# Optimizing a Trainium2 kernel written in Bass

```python
import math
import jax, jax.numpy as jnp
from jax import lax
import numpy as np

D_MODEL = 1024
BATCH = 1
SEQ = 1024
DEPTH = 1

CHUNK = 64
D_MIX = D_MODEL
D_CONV = D_MIX // 2
CONV_GROUPS = 8
CONV_WIDTH = 31
HEAD_DIM = 64
N_HEADS = (D_MIX - D_CONV) // HEAD_DIM
N_KV = 2
GROUP = N_HEADS // N_KV
WINDOW = 128
WINDOW_CHUNKS = WINDOW // CHUNK
IN_COLS = 2 * D_CONV + N_HEADS * HEAD_DIM + 2 * N_KV * HEAD_DIM
N_EXPERTS = 32
TOP_K = 4
D_FF = D_MODEL
SWIGLU_LIMIT = 7.0
SWIGLU_ALPHA = 1.702
EXPERT_BLOCK = 128
EPS = 1e-5

kernel_name = "hybrid_conformer_swa_sink_moe_block"

def rms_norm(x, g):
    xf = x.astype(jnp.float32)
    y = xf * lax.rsqrt(jnp.mean(xf * xf, axis=-1, keepdims=True) + EPS)
    return (y * g.astype(jnp.float32)).astype(x.dtype)

def layer_norm(x, g, b):
    xf = x.astype(jnp.float32)
    mu = jnp.mean(xf, axis=-1, keepdims=True)
    var = jnp.mean(jnp.square(xf - mu), axis=-1, keepdims=True)
    y = (xf - mu) * lax.rsqrt(var + EPS)
    return (y * g.astype(jnp.float32) + b.astype(jnp.float32)).astype(x.dtype)

def conformer_conv_group(a, conv_w, conv_b, ln_g, ln_b):
    val, gate = a[..., :D_CONV], a[..., D_CONV:]
    z = val * jax.nn.sigmoid(gate)
    z = lax.conv_general_dilated(
        z, conv_w[:, None, :].astype(z.dtype), window_strides=(1,),
        padding=[(CONV_WIDTH - 1, 0)],
        dimension_numbers=("NWC", "WIO", "NWC"),
        feature_group_count=D_CONV) + conv_b
    z = layer_norm(z, ln_g, ln_b)
    return jax.nn.silu(z)

def swa_sink_attention(q, k, v, q_norm_g, k_norm_g, sinks):
    B, S, _ = q.shape
    NC = S // CHUNK
    q = rms_norm(q.reshape(B, S, N_HEADS, HEAD_DIM), q_norm_g)
    k = rms_norm(k.reshape(B, S, N_KV, HEAD_DIM), k_norm_g)
    q = q.reshape(B, NC, CHUNK, N_KV, GROUP, HEAD_DIM)
    k = k.reshape(B, NC, CHUNK, N_KV, HEAD_DIM)
    v = v.reshape(B, NC, CHUNK, N_KV, HEAD_DIM)

    def band(t):
        parts = []
        for j in range(WINDOW_CHUNKS - 1, -1, -1):
            shifted = jnp.concatenate([jnp.zeros_like(t[:, :j]), t[:, :NC - j]], axis=1) if j > 0 else t
            parts.append(shifted)
        return jnp.concatenate(parts, axis=2)

    kb, vb = band(k), band(v)
    scale = 1.0 / math.sqrt(HEAD_DIM)
    s = jnp.einsum("bnqhgd,bnkhd->bnhgqk", q, kb,
                   preferred_element_type=jnp.float32) * scale
    chunk_id = jnp.arange(NC)[:, None]
    key_chunk_offset = (WINDOW_CHUNKS - 1) - jnp.arange(WINDOW)[None, :] // CHUNK
    valid = chunk_id >= key_chunk_offset
    s = jnp.where(valid[None, :, None, None, None, :], s, jnp.finfo(jnp.float32).min)
    sink = sinks.astype(jnp.float32).reshape(N_KV, GROUP)[None, None, :, :, None, None]
    m = jnp.maximum(jnp.max(s, axis=-1, keepdims=True), sink)
    e = jnp.exp(s - m)
    p = e / (jnp.sum(e, axis=-1, keepdims=True) + jnp.exp(sink - m))
    o = jnp.einsum("bnhgqk,bnkhd->bnqhgd", p.astype(vb.dtype), vb)
    return o.reshape(B, S, N_HEADS * HEAD_DIM)

def clamped_swiglu_expert(xb, w1, b1, w2, b2):
    h = xb @ w1 + b1
    x_glu = jnp.minimum(h[..., :D_FF], SWIGLU_LIMIT)
    x_lin = jnp.clip(h[..., D_FF:], -SWIGLU_LIMIT, SWIGLU_LIMIT)
    act = x_glu * jax.nn.sigmoid(SWIGLU_ALPHA * x_glu) * (x_lin + 1.0)
    return act @ w2 + b2

def moe(xf, router_w, router_b, w1, b1, w2, b2):
    T, D = xf.shape
    logits = (xf @ router_w).astype(jnp.float32) + router_b.astype(jnp.float32)
    top_val, top_idx = lax.top_k(logits, TOP_K)
    gates = jax.nn.softmax(top_val, axis=-1)
    A = T * TOP_K
    e_flat = top_idx.reshape(A)
    order = jnp.argsort(e_flat, stable=True)
    e_sorted = e_flat[order]
    counts = jnp.bincount(e_flat, length=N_EXPERTS)
    start = jnp.cumsum(counts) - counts
    padded = (counts + EXPERT_BLOCK - 1) // EXPERT_BLOCK * EXPERT_BLOCK
    pad_end = jnp.cumsum(padded)
    pad_start = pad_end - padded
    dest_sorted = pad_start[e_sorted] + (jnp.arange(A) - start[e_sorted])
    n_blocks = -(-A // EXPERT_BLOCK) + N_EXPERTS
    P = n_blocks * EXPERT_BLOCK
    slot_token = jnp.zeros((P,), jnp.int32).at[dest_sorted].set((order // TOP_K).astype(jnp.int32))
    block_expert = jnp.minimum(
        jnp.searchsorted(pad_end, jnp.arange(n_blocks) * EXPERT_BLOCK, side="right"),
        N_EXPERTS - 1)

    def run_block(args):
        tok, e = args
        return clamped_swiglu_expert(xf[tok], w1[e], b1[e], w2[e], b2[e])

    ys = lax.map(run_block, (slot_token.reshape(n_blocks, EXPERT_BLOCK), block_expert))
    ys = ys.reshape(P, D)
    dest = jnp.zeros((A,), jnp.int32).at[order].set(dest_sorted.astype(jnp.int32))
    y_assign = ys[dest].reshape(T, TOP_K, D)
    return jnp.einsum("tk,tkd->td", gates.astype(y_assign.dtype), y_assign)

def setup_inputs(seed: int = 0) -> dict:
    key = jax.random.key(seed)
    ks = jax.random.split(key, 20)
    f32 = jnp.float32
    nrm = lambda k, shape, s: jax.random.normal(k, shape, f32) * s
    return {
        "x": nrm(ks[0], (BATCH, SEQ, D_MODEL), 1.0),
        "norm1_g": 1.0 + nrm(ks[1], (D_MODEL,), 0.02),
        "w_in": nrm(ks[2], (D_MODEL, IN_COLS), D_MODEL ** -0.5),
        "conv_w": nrm(ks[3], (CONV_WIDTH, D_CONV), CONV_WIDTH ** -0.5),
        "conv_b": nrm(ks[4], (D_CONV,), 0.02),
        "conv_ln_g": 1.0 + nrm(ks[5], (D_CONV,), 0.02),
        "conv_ln_b": nrm(ks[6], (D_CONV,), 0.02),
        "q_norm_g": 1.0 + nrm(ks[7], (HEAD_DIM,), 0.02),
        "k_norm_g": 1.0 + nrm(ks[8], (HEAD_DIM,), 0.02),
        "sinks": nrm(ks[9], (N_HEADS,), 1.0),
        "w_out": nrm(ks[10], (D_MIX, D_MODEL), D_MIX ** -0.5),
        "norm2_g": 1.0 + nrm(ks[11], (D_MODEL,), 0.02),
        "router_w": nrm(ks[12], (D_MODEL, N_EXPERTS), D_MODEL ** -0.5),
        "router_b": nrm(ks[13], (N_EXPERTS,), 0.01),
        "w1": nrm(ks[14], (N_EXPERTS, D_MODEL, 2 * D_FF), D_MODEL ** -0.5),
        "b1": nrm(ks[15], (N_EXPERTS, 2 * D_FF), 0.02),
        "w2": nrm(ks[16], (N_EXPERTS, D_FF, D_MODEL), D_FF ** -0.5),
        "b2": nrm(ks[17], (N_EXPERTS, D_MODEL), 0.02),
    }

def reference(x, norm1_g, w_in, conv_w, conv_b, conv_ln_g, conv_ln_b, q_norm_g,
              k_norm_g, sinks, w_out, norm2_g, router_w, router_b, w1, b1, w2, b2):
    B, S, D = x.shape
    h = x
    for _ in range(DEPTH):
        u = rms_norm(h, norm1_g)
        proj = u @ w_in
        c0 = 2 * D_CONV
        c1 = c0 + N_HEADS * HEAD_DIM
        c2 = c1 + N_KV * HEAD_DIM
        conv_out = conformer_conv_group(proj[..., :c0], conv_w, conv_b, conv_ln_g, conv_ln_b)
        attn_out = swa_sink_attention(proj[..., c0:c1], proj[..., c1:c2], proj[..., c2:],
                                      q_norm_g, k_norm_g, sinks)
        mixed = jnp.concatenate([conv_out, attn_out], axis=-1)
        h = h + mixed @ w_out
        v = rms_norm(h, norm2_g).reshape(B * S, D)
        h = h + moe(v, router_w, router_b, w1, b1, w2, b2).reshape(B, S, D)
    return h


_drawn_inputs = setup_inputs


def setup_inputs(seed=0):
    import zlib

    import numpy as np

    out = dict(_drawn_inputs(seed))
    spreads = {}
    factors = {'q_norm_g': 6.055, 'k_norm_g': 3.577, 'sinks': 4.121, 'b1': 5.498, 'b2': 6.289}
    for name, (base, spread) in spreads.items():
        noise = np.random.default_rng([zlib.crc32(name.encode()), seed]).standard_normal(out[name].shape)
        drawn = base * np.exp(spread * noise) if base else spread * noise
        out[name] = __import__('jax').numpy.asarray(drawn.astype(out[name].dtype))
    for name, factor in factors.items():
        out[name] = (out[name] * factor).astype(out[name].dtype)
    return out
```

```python
from contextlib import ExitStack

import numpy as np
import concourse.bass as bass
from concourse import mybir

P = 128
SEQ, D = 1024, 1024
NT = SEQ // P
KD = D // P
D_CONV, WIDTH = 512, 31
CT = D_CONV // P
PAD = WIDTH - 1
HD, NH, NKV = 64, 8, 2
GROUP = NH // NKV
QKV = NH * HD + 2 * NKV * HD
CHUNK = 64
WIN = 3 * CHUNK
NE, TOPK, FF = 32, 4, 1024
MT = FF // P
SLOTS = 256
TIERS = [*range(96, 160, 4), 160, 168, 176, 192, 216, 256]
QMAX = NE + SEQ * TOPK // SLOTS
ROW = D + NE
LIMIT, ALPHA, EPS = 7.0, 1.702, 1e-5
NEG = -1.0e30
HALF = 512


def hybrid_block(nc, x, norm1_g, w_in, conv_w, conv_b, conv_ln_g, conv_ln_b, q_norm_g, k_norm_g, sinks,
                 w_out, norm2_g, router_w, router_b, w1, b1, w2, b2, out):
    f32, bf16, i32, u32 = mybir.dt.float32, mybir.dt.bfloat16, mybir.dt.int32, mybir.dt.uint32
    ALU, ACT, AX = mybir.AluOpType, mybir.ActivationFunctionType, mybir.AxisListType
    ds = bass.ds

    x2 = x.rearrange("b s d -> (b s) d")
    out2 = out.rearrange("b s d -> (b s) d")
    rows_d = nc.dram_tensor("token_rows", [SEQ, ROW], f32, kind="Internal").ap()

    with ExitStack() as ctx:
        ctx.enter_context(nc.allow_non_contiguous_dma(reason="small constants"))

        def sb(name, shape, dt=f32):
            return ctx.enter_context(nc.sbuf_tensor(name, shape, dt))

        def sem(name):
            return ctx.enter_context(nc.semaphore(name))

        KW = 256
        arena = sb("arena", [P, 184 * KW + 192])

        def part(kib, *shape):
            at = int(kib * KW)
            n = int(np.prod(shape))
            flat = arena[:, at:at + n]
            if len(shape) == 1:
                return flat
            if len(shape) == 2:
                return flat.rearrange("p (a b) -> p a b", a=shape[0])
            return flat.rearrange("p (a b c) -> p a b c", a=shape[0], b=shape[1])

        w1_sb = part(0, KD, 2 * FF)
        w2_sb = part(64, MT, D)
        xT = part(96, KD, SLOTS)
        act = part(104, MT, SLOTS)
        yT = part(112, KD, SLOTS)
        g1 = part(120, 2, SLOTS)
        sg = part(122, 2, SLOTS)
        l1 = part(124, 2, SLOTS)
        tt = part(126, 2, SLOTS)
        gath = part(128, 2, ROW)
        ytok = part(144.5, 2, D)
        zeros = part(140, D)[0:2, :]
        onehot = part(152.5, 1024).bitcast(bf16).rearrange("p (t s) -> p t s", t=NT)
        qs = part(0, QKV - NKV * HD)
        sq = part(2.5, QKV - NKV * HD)
        qn = part(5, GROUP + 1, NKV, HD)
        qT = part(7.5, GROUP, P)
        S = part(9.5, NH, WIN)
        prob = part(15.5, NH, SLOTS)
        PTc = part(23.5, NH, P)
        PTp = part(27.5, NH, CHUNK)
        mask_first = part(29.5, WIN)
        mask_rest = part(30.25, WIN)
        w_qkv = part(32, KD, QKV)
        sigb = part(56, 2, HALF)
        valb = part(60, 2, HALF)
        tapped = [part(9.5, SEQ), part(23.5, SEQ)]
        w_cv = part(64, KD, 2 * D_CONV)
        w_o = part(64, KD, D)
        uT = part(96, KD, SEQ)
        hb = part(96, 4, D)
        vrow = part(112, 2, ROW)
        zT = part(128, CT, PAD + SEQ)
        sqT = part(128, CT, SEQ)
        xh = part(128, 2, D)
        vT = part(136, KD, P)
        sqx = part(24, D)
        sigl = part(121, 2, HALF)
        hsq = part(121, D)
        cT = part(144.5, CT, SEQ)
        aT = part(160.5, CT, SEQ)
        xin = part(144.5, NT, D)
        kT = part(176.5, CHUNK + SEQ)
        vv = part(176.5 + 4.25, NT, P)
        rows30 = part(56, P)
        rows_cw = part(56.5, D_CONV)
        rows_b1 = part(13.5, 4, P)
        b2_sb = part(140, D)[0:NE, :]
        rln = part(96, 2, HALF)

        ident = sb("ident", [P, P])
        ones_f = sb("ones_f", [P, P])
        ones_ln = sb("ones_ln", [P, P])
        ones_b = sb("ones_b", [P, P], bf16)
        tri_b = sb("tri_b", [P, P], bf16)
        iota_s = sb("iota_s", [P, SLOTS], bf16)
        iota_e = sb("iota_e", [P, NE])
        tokcode = sb("tokcode", [P, NT, 2], bf16)
        tokid = sb("tokid", [P, NT])
        qcol = sb("qcol", [P, 1])
        cols = sb("cols", [P, 32 + CT * WIDTH])
        b1T = sb("b1T", [P, NE * 2 * MT])
        rw = sb("rw", [P, KD, NE])
        sink = sb("sink", [P, NH])
        rb = sb("rb", [P, NE])
        mhalf = sb("mhalf", [P, 16])
        ss = sb("ss", [P, 3, 16])
        rs = sb("rs", [P, 3, 16])
        mx = sb("mx", [P, NH])
        nmx = sb("nmx", [P, NH])
        sd = sb("sd", [P, NH])
        es = sb("es", [P, NH])
        den = sb("den", [P, NH])
        rden = sb("rden", [P, NH])
        lg = sb("lg", [P, NE])
        top8 = sb("top8", [P, 8])
        ix8 = sb("ix8", [P, 8], u32)
        ixf = sb("ixf", [P, 8])
        mk = sb("mk", [P, 2, NE])
        eg = sb("eg", [P, NE])
        gg = sb("gg", [P, NE])
        gs = sb("gs", [P, 4])
        GT = sb("GT", [NE, P])
        Mb = sb("Mb", [P, NT, NE], bf16)
        Mf = sb("Mf", [P, NT, NE])
        pos = sb("pos", [P, NT, NE])
        nE = sb("nE", [P, NE])
        rka = sb("rka", [P, NT, NE])
        rkd = sb("rkd", [P, NT, NE])
        rank = sb("rank", [P, NT, NE])
        cum = sb("cum", [P, 2, 16 + NE])
        tb = sb("tb", [P, 3, NE])
        tc = sb("tc", [P, 8])
        limits = sb("limits", [P, len(TIERS) - 1])
        diag = sb("diag", [P, 3, 64])
        tabI = sb("tabI", [P, 144], i32)
        baseB = sb("baseB", [P, 64])
        r8 = sb("r8", [P, NT])
        idf = sb("idf", [P, 4])
        idx_next = sb("idx_next", [P, 2], i32)
        first_rows = sb("first_rows", [2, 2], i32)
        idx_cur = sb("idx_cur", [P, 2], i32)
        gate_cur = sb("gate_cur", [P, 2])
        b1c = sb("b1c", [P, 2 * MT])

        G1, G2, CB, LG, LB, QG, KG, CW = 0, 8, 16, 20, 24, 28, 29, 32

        def col(c):
            return cols[:, c:c + 1]

        bank = [ctx.enter_context(nc.psum_tensor(f"bank{b}", [P, HALF], f32)) for b in range(8)]

        x_in = [sem(f"x_in{t}") for t in range(NT)]
        wcv_in, wqkv_in, wo_in = sem("wcv_in"), sem("wqkv_in"), sem("wo_in")
        tap_ready, tap_added = sem("tap_ready"), sem("tap_added")
        rows_in, small_in = sem("rows_in"), sem("small_in")
        xh_in = [sem(f"xh_in{i}") for i in range(2)]
        b2_in, ident_ready, consts = sem("b2_in"), sem("ident_ready"), sem("consts")
        cols_mm, cols_done, b1_mm, b1_done = sem("cols_mm"), sem("cols_done"), sem("b1_mm"), sem("b1_done")
        xsq, xss, xrs, u_ready = sem("xsq"), sem("xss"), sem("xrs"), sem("u_ready")
        ut_mm, ut_act, ut_dve = sem("ut_mm"), sem("ut_act"), sem("ut_dve")
        glu_mm, glu_ev, z_ready = sem("glu_mm"), sem("glu_ev"), sem("z_ready")
        q_mm, kv_mm, q_ev, kv_ev = sem("q_mm"), sem("kv_mm"), sem("q_ev"), sem("kv_ev")
        hss, hrs, qn_ready = sem("hss"), sem("hrs"), sem("qn_ready")
        qt_mm, qt_ev, s_mm, s_ev = sem("qt_mm"), sem("qt_ev"), sem("s_mm"), sem("s_ev")
        m_ready, e_ready, p_ready = sem("m_ready"), sem("e_ready"), sem("p_ready")
        pt_mm, pt_ev, o_mm, o_ev = sem("pt_mm"), sem("pt_ev"), sem("o_mm"), sem("o_ev")
        conv_done, mean_mm, cen_done, csq_done, var_mm = (sem(n) for n in (
            "conv_done", "mean_mm", "cen_done", "csq_done", "var_mm"))
        lvar, lrs, cn_done, sil_act, mix_ready = (sem(n) for n in (
            "lvar", "lrs", "cn_done", "sil_act", "mix_ready"))
        wo_mm, h_ready, h_sq, h_rs, v_ready = (sem(n) for n in ("wo_mm", "h_ready", "h_sq", "h_rs", "v_ready"))
        vt_mm, vt_ev, lg_mm, lg_neg, eg_ready, gate_ready, mask_ready = (sem(n) for n in (
            "vt_mm", "vt_ev", "lg_mm", "lg_neg", "eg_ready", "gate_ready", "mask_ready"))
        gt_mm, gt_ev, b2_mm, h2_ready = sem("gt_mm"), sem("gt_ev"), sem("b2_mm"), sem("h2_ready")
        row_out = [sem(f"row_out{i}") for i in range(2)]
        h_out = [sem(f"h_out{i}") for i in range(4)]
        rank_mm, diag_ready, tab_mm, tab_ready = (sem(n) for n in ("rank_mm", "diag_ready", "tab_mm", "tab_ready"))
        w1_in = [sem(f"w1_in{c}") for c in range(4)]
        w2_in = [sem(f"w2_in{c}") for c in range(2)]
        oh_ready, idx_mm, idx_ready, gath_in = sem("oh_ready"), sem("idx_mm"), sem("idx_ready"), sem("gath_in")
        xt_mm, xt_ev, cur_ready = sem("xt_mm"), sem("xt_ev"), sem("cur_ready")
        hid_mm, hid_free, g1_ready, sg_ready, sg_free, act_ready = (sem(n) for n in (
            "hid_mm", "hid_free", "g1_ready", "sg_ready", "sg_free", "act_ready"))
        y_mm, yT_ev, yt_mm, yt_ev = sem("y_mm"), sem("yT_ev"), sem("yt_mm"), sem("yt_ev")
        added = [sem(f"added{i}") for i in range(2)]
        pool_past = sem("pool_past")
        dve_own, act_own, pool_own, dve_loop = sem("dve_own"), sem("act_own"), sem("pool_own"), sem("dve_loop")

        FIRST_TAPS = [(1 + 5 * max(i - 2, 0), 1 + 5 * max(i - 1, 0)) for i in range(2 * CT)]
        assert FIRST_TAPS[-1][1] == WIDTH
        N_ROWS, N_SMALL = 10, 4
        ATTN = range(NT)
        block = ctx.enter_context(nc.Block())

        def store_rows(sp, t):
            sp.wait_ge(gate_ready, t + 1)
            sp.dma_start(rows_d[t * P:(t + 1) * P, :], vrow[:, t % 2, :]).then_inc(row_out[t % 2], 16)
            sp.wait_ge(h2_ready, t + 1)
            sp.dma_start(out2[t * P:(t + 1) * P, :], hb[:, t % 4, :]).then_inc(h_out[t % 4], 16)

        def expert(w, e):
            return w[e] if isinstance(e, int) else w[ds(e, 1), :, :].rearrange("e a b -> (e a) b")

        def load_w1(sp, c, e):
            src = expert(w1, e)
            for side in range(2):
                lo = side * FF + c * 256
                sp.dma_start(w1_sb[:, :, lo:lo + 256],
                             src[:, lo:lo + 256].rearrange("(k p) n -> p k n", p=P)).then_inc(w1_in[c], 16)

        def load_w2(sp, c, e):
            src = expert(w2, e)
            sp.dma_start(w2_sb[:, :, c * HALF:(c + 1) * HALF],
                         src[:, c * HALF:(c + 1) * HALF].rearrange("(k p) n -> p k n", p=P)).then_inc(w2_in[c], 16)

        @block.sync
        def _(sp):
            for t in range(NT):
                sp.dma_start(xin[:, t, :], x2[t * P:(t + 1) * P, :]).then_inc(x_in[t], 16)
            sp.wait_ge(rows_in, 16 * N_ROWS)
            for h in range(2):
                sp.dma_start(w_cv[:, 4 * h:4 * h + 4, :],
                             w_in[512 * h:512 * h + 512, 0:2 * D_CONV].rearrange("(k p) n -> p k n", p=P)
                             ).then_inc(wcv_in, 16)
            sp.dma_start(w_qkv, w_in[:, 2 * D_CONV:].rearrange("(k p) n -> p k n", p=P)).then_inc(wqkv_in, 16)
            sp.wait_ge(glu_mm, 2 * CT)
            sp.dma_start(w_o[:, 0:CT, :], w_out[0:D_CONV, :].rearrange("(k p) n -> p k n", p=P)).then_inc(wo_in, 16)
            for g in range(NKV):
                lo = D_CONV + g * GROUP * HD
                sp.dma_start(w_o[g * HD:(g + 1) * HD, CT:KD, :],
                             w_out[lo:lo + GROUP * HD, :].rearrange("(j p) n -> p j n", p=HD)).then_inc(wo_in, 16)
            sp.wait_ge(pt_ev, 3 * NT)
            sp.wait_ge(o_mm, NT)
            sp.wait_ge(z_ready, 2 * CT)
            for c in range(4):
                load_w1(sp, c, 0)
            sp.wait_ge(var_mm, 2)
            sp.dma_start(b2_sb, b2).then_inc(b2_in, 16)
            for t in range(NT):
                if t >= 2:
                    sp.wait_ge(h_ready, t - 1)
                sp.dma_start(xh[:, t % 2, :], x2[t * P:(t + 1) * P, :]).then_inc(xh_in[t % 2], 16)
                if t >= 2:
                    store_rows(sp, t - 2)
            for t in range(NT - 2, NT):
                store_rows(sp, t)
            sp.wait_ge(wo_mm, 2 * NT)
            for c in range(2):
                load_w2(sp, c, 0)
            sp.wait_ge(tab_ready, 1)
            n_pass = sp.value_load(tabI[0:1, 128:129], min_val=NE, max_val=QMAX)
            with sp.Fori(1, n_pass) as q:
                e = sp.value_load(tabI[0:1, ds(q, 1)], min_val=0, max_val=NE - 1)
                for c in range(4):
                    sp.wait_ge(hid_mm, q * MT + (2 * c + 2 - MT))
                    load_w1(sp, c, e)
                for c in range(2):
                    sp.wait_ge(y_mm, q * KD + (4 * c + 4 - KD))
                    load_w2(sp, c, e)

        def mixed_bank(t):
            return 4 if t == 0 else 2 * (t % 2)

        def by_tier(eng, tier, body, lo=0, hi=len(TIERS)):
            if hi - lo == 1:
                body(TIERS[lo])
                return
            mid = (lo + hi) // 2
            with eng.If(tier < mid):
                by_tier(eng, tier, body, lo, mid)
            with eng.Else():
                by_tier(eng, tier, body, mid, hi)

        def gather(pool, n):
            pool.wait_ge(idx_ready, n)
            pool.sem_inc(pool_past, 1)
            for h in range(2):
                pool.indirect_dma_start(out=gath[:, h, :], out_offset=None, in_=rows_d,
                                        in_offset=bass.IndirectOffsetOnAxis(ap=idx_next[:, h:h + 1], axis=0)
                                        ).then_inc(gath_in, 16)

        def add_rows(pool, h, n, rows=None):
            pool.indirect_dma_start(out=out2, out_offset=bass.IndirectOffsetOnAxis(ap=idx_cur[0:n, h:h + 1], axis=0),
                                    in_=ytok[0:n, h, :] if rows is None else rows, in_offset=None, compute_op=ALU.add).then_inc(added[h], 16)

        def add_pass(pool, n):
            add_rows(pool, 0, min(n, P))
            if n > P:
                add_rows(pool, 1, n - P)
            else:
                add_rows(pool, 1, 2, zeros)

        @block.gpsimd
        def _(pool):
            own = [0]

            def link(ins):
                own[0] += 1
                ins.then_inc(pool_own, 1)
                pool.wait_ge(pool_own, own[0])

            def rsqrt_mean(dst, src, n, done):
                w = src.shape[-1]
                link(pool.tensor_scalar(src, src, 1.0 / n, EPS, ALU.mult, ALU.add))
                pool.tensor_tensor(dst, src, mhalf[:, 0:w], ALU.pow).then_inc(done, 1)

            link(pool.memset(ident[:], 0.0))
            link(pool.affine_select(out=ident[:], in_=ident[:], compare_op=ALU.not_equal, fill=1.0, base=0,
                                    pattern=[[-1, P]], channel_multiplier=1))
            pool.sem_inc(ident_ready, 1)
            link(pool.memset(mhalf[:, 0:16], -0.5))
            link(pool.memset(zT[:, :, 0:PAD], 0.0))
            for t in range(NT):
                pool.wait_ge(xss, t + 1)
                rsqrt_mean(rs[:, 0, t:t + 1], ss[:, 0, t:t + 1], D, xrs)
            link(pool.memset(ones_f[:], 1.0))
            link(pool.memset(ones_ln[:], 1.0 / D_CONV))
            link(pool.memset(ones_b[:], 1.0))
            link(pool.affine_select(out=tri_b[:], in_=ones_b[:], compare_op=ALU.is_gt, fill=0.0, base=0,
                                    pattern=[[1, P]], channel_multiplier=-1))
            link(pool.memset(kT[:, 0:CHUNK], 0.0))
            link(pool.memset(prob, 0.0))
            link(pool.memset(mask_rest, 0.0))
            for lo, base, step in ((0, 2 * CHUNK - 1, -1), (CHUNK, -CHUNK, 1)):
                link(pool.affine_select(out=mask_rest[lo:lo + CHUNK, :], in_=mask_rest[lo:lo + CHUNK, :],
                                        compare_op=ALU.is_ge, fill=NEG, base=base, pattern=[[step, WIN]],
                                        channel_multiplier=0))
            link(pool.affine_select(out=mask_first, in_=mask_rest, compare_op=ALU.is_ge, fill=NEG, base=-CHUNK,
                                    pattern=[[1, WIN]], channel_multiplier=0))
            for dst, pattern, cm in ((iota_s[:], [[1, SLOTS]], 0), (iota_e[:], [[1, NE]], 0),
                                     (tokcode[:, :, 0], [[1, NT]], 0), (tokcode[:, :, 1], [[0, NT]], 1),
                                     (tokid[:], [[P, NT]], 1), (qcol[:], [[0, 1]], 1)):
                link(pool.iota(dst, pattern=pattern, base=0, channel_multiplier=cm,
                               allow_small_or_imprecise_dtypes=True))
            for i, n in enumerate(TIERS[:-1]):
                pool.memset(limits[:, i:i + 1], float(n))
            link(pool.iota(first_rows[:], pattern=[[2, 2]], base=0, channel_multiplier=1))
            pool.sem_inc(consts, 1)

            def glu(i):
                pool.wait_ge(glu_ev, 2 * (i + 1))
                c, h = divmod(i, 2)
                pool.tensor_tensor(zT[:, c, PAD + h * HALF:PAD + (h + 1) * HALF], sigb[:, i % 2, :],
                                   valb[:, i % 2, :], ALU.mult).then_inc(z_ready, 1)

            for i in range(2 * CT):
                glu(i)
                for j in range(*FIRST_TAPS[i]):
                    pool.wait_ge(tap_ready, j + 1)
                    if j >= 2:
                        pool.wait_ge(tap_added, j - 1)
                    pool.tensor_tensor(cT[:, 0, :], cT[:, 0, :], tapped[j % 2], ALU.add).then_inc(tap_added, 1)
            for s in range(NT):
                pool.wait_ge(hss, s + 1)
                if s >= 1:
                    pool.wait_ge(qn_ready, s)
                rsqrt_mean(rs[:, 1, 0:10], ss[:, 1, 0:10], HD, hrs)
            for t in range(NT):
                pool.wait_ge(h_sq, t + 1)
                rsqrt_mean(rs[:, 2, t:t + 1], ss[:, 2, t:t + 1], D, h_rs)

            for i in range(2):
                pool.wait_ge(row_out[i], 16 * (NT // 2))
            gather(pool, 1)
            for i in range(4):
                pool.wait_ge(h_out[i], 16 * (NT // 4))
            pool.wait_ge(b2_mm, NT)
            link(pool.memset(zeros, 0.0))
            for i in range(2):
                pool.indirect_dma_start(out=out2, out_offset=bass.IndirectOffsetOnAxis(ap=first_rows[:, i:i + 1], axis=0),
                                        in_=zeros, in_offset=None, compute_op=ALU.add).then_inc(added[i], 16)
            pool.wait_ge(tab_ready, 1)
            n_pass = pool.value_load(tabI[0:1, 128:129], min_val=NE, max_val=QMAX)
            with pool.Fori(0, n_pass) as q:
                tier = pool.value_load(tabI[0:1, ds(q + 64, 1)])
                pool.wait_ge(cur_ready, q + 1)
                pool.wait_ge(xt_mm, q * 4 + 4)
                gather(pool, q + 2)
                pool.wait_ge(yt_ev, q * 2 + 2)
                for i in range(2):
                    pool.wait_ge(added[i], q * 16 + 16)
                pool.sem_inc(pool_past, 1)
                by_tier(pool, tier, lambda n: add_pass(pool, n))
            for i in range(2):
                pool.wait_ge(added[i], n_pass * 16 + 16)

        def act_pass(a, q, n):
            q8 = a.snap(q * 8)
            q2 = a.snap(q * 2)
            for m in range(MT):
                a.wait_ge(g1_ready, q8 + m + 1)
                a.wait_ge(sg_free, q8 + m + 1)
                a.activation(sg[:, m % 2, 0:n], g1[:, m % 2, 0:n], ACT.Sigmoid, scale=ALPHA).then_inc(sg_ready, 1)

            def take_yT(d):
                a.wait_ge(y_mm, q8 + d + 1)
                a.activation(yT[:, d, 0:n], bank[2 + d % 2][:, 0:n], ACT.Copy).then_inc(yT_ev, 1)

            def take_y(b):
                a.wait_ge(yt_mm, q2 + b + 1)
                if b == 0:
                    a.wait_ge(cur_ready, q + 1)
                    for i in range(2):
                        a.wait_ge(added[i], q * 16 + 16)
                lo = b * HALF
                w = min(n, P)
                last = a.activation(ytok[0:w, 0, lo:lo + HALF], bank[4 + b][0:w, :], ACT.Copy,
                                    scale=gate_cur[0:w, 0:1])
                if n > P:
                    last = a.activation(ytok[0:n - P, 1, lo:lo + HALF], bank[7][0:n - P, :], ACT.Copy,
                                        scale=gate_cur[0:n - P, 1:2])
                last.then_inc(yt_ev, 1)

            for d in range(6):
                take_yT(d)
            take_y(0)
            take_yT(6)
            take_yT(7)
            take_y(1)

        @block.scalar
        def _(a):
            own = [0]

            def link(ins):
                own[0] += 1
                ins.then_inc(act_own, 1)
                a.wait_ge(act_own, own[0])

            def rows(v, n):
                return v.rearrange("(r c) -> r c", r=n)

            as_rows = [(rows30[0:8, :], rows(norm1_g, 8)), (rows30[8:16, :], rows(norm2_g, 8)),
                       (rows30[16:20, :], rows(conv_b, 4)), (rows30[20:24, :], rows(conv_ln_g, 4)),
                       (rows30[24:28, :], rows(conv_ln_b, 4)),
                       (rows30[28:29, 0:HD], rows(q_norm_g, 1)), (rows30[28:29, HD:P], rows(q_norm_g, 1)),
                       (rows30[29:30, 0:HD], rows(k_norm_g, 1)), (rows30[29:30, HD:P], rows(k_norm_g, 1)),
                       (rows_cw[0:WIDTH, :], conv_w)]
            small = [(rows_b1, b1.rearrange("e (m c) -> (e m) c", c=P).rearrange("(g r) c -> r g c", r=P)),
                     (rw[:], router_w.rearrange("(k p) e -> p k e", p=P)),
                     (sink[:], rows(sinks, 1).to_broadcast([P, NH])),
                     (rb[:], rows(router_b, 1).to_broadcast([P, NE]))]
            assert len(as_rows) == N_ROWS and len(small) == N_SMALL
            for dst, src in as_rows:
                a.dma_start(dst, src).then_inc(rows_in, 16)

            for t in range(NT):
                a.wait_ge(x_in[t], 16)
                if t >= 1:
                    a.wait_ge(xss, t)
                a.activation(sqx, xin[:, t, :], ACT.Square, accum_out=ss[:, 0, t:t + 1]).then_inc(xss, 1)
            for dst, src in small:
                a.dma_start(dst, src).then_inc(small_in, 16)
            a.wait_ge(cols_done, 1)
            for g in range(0, 2 * KD, 2):
                h, k = divmod(g, KD)
                a.wait_ge(ut_mm, g + 1)
                a.activation(uT[:, k, h * HALF:(h + 1) * HALF], bank[6][:], ACT.Copy, scale=col(G1 + k)
                             ).then_inc(ut_act, 1)
            for i in range(2 * CT):
                a.wait_ge(glu_mm, i + 1)
                if i >= 2:
                    a.wait_ge(z_ready, i - 1)
                a.activation(sigb[:, i % 2, :], bank[2 * (i % 2) + 1][:], ACT.Sigmoid).then_inc(glu_ev, 1)
                a.activation(valb[:, i % 2, :], bank[2 * (i % 2)][:], ACT.Copy).then_inc(glu_ev, 1)
                for j in range(*FIRST_TAPS[i]):
                    z = zT[:, 0, j:j + SEQ]
                    if j == 1:
                        a.wait_ge(z_ready, 2)
                        a.activation(cT[:, 0, :], zT[:, 0, 0:SEQ], ACT.Identity, scale=col(CW), bias=col(CB)
                                     ).then_inc(tap_ready, 1)
                    if j >= 3:
                        a.wait_ge(tap_added, j - 2)
                    a.activation(tapped[j % 2], z, ACT.Copy, scale=col(CW + j)).then_inc(tap_ready, 1)

            def take_q(s):
                a.wait_ge(q_mm, s + 1)
                a.activation(qs[:, 0:HALF], bank[4][:], ACT.Copy)
                a.activation(sq[:, 0:HALF], bank[4][:], ACT.Square).then_inc(q_ev, 1)

            def take_kv(s):
                a.wait_ge(kv_mm, s + 1)
                if s >= 1:
                    a.wait_ge(qn_ready, s)
                a.activation(qs[:, HALF:HALF + P], bank[5][:, 0:P], ACT.Copy)
                a.activation(sq[:, HALF:HALF + P], bank[5][:, 0:P], ACT.Square)
                a.activation(vv[:, s, :], bank[5][:, P:2 * P], ACT.Copy).then_inc(kv_ev, 1)

            def take_qT(s):
                a.wait_ge(qt_mm, s + 1)
                a.activation(qT, bank[6][:].rearrange("p (j q) -> p j q", j=GROUP), ACT.Copy, scale=col(QG))
                a.activation(kT[:, CHUNK + s * P:CHUNK + (s + 1) * P], bank[7][:, 0:P], ACT.Copy, scale=col(KG)
                             ).then_inc(qt_ev, 1)

            def exps(s):
                a.wait_ge(m_ready, s + 1)
                for h in range(NH):
                    a.activation(S[:, h, :], S[:, h, :], ACT.Exp, bias=nmx[:, h:h + 1], accum_out=den[:, h:h + 1])
                a.activation(es[:], sd[:], ACT.Exp).then_inc(e_ready, 1)

            def take_PT(s):
                for g in range(NKV):
                    a.wait_ge(pt_mm, 3 * s + g + 1)
                    a.activation(PTc[:, g * GROUP:(g + 1) * GROUP, :],
                                 bank[g][:].rearrange("p (j q) -> p j q", j=GROUP), ACT.Copy).then_inc(pt_ev, 1)
                a.wait_ge(pt_mm, 3 * s + 3)
                a.activation(PTp, bank[2][:].rearrange("p (j q) -> p j q", j=NH), ACT.Copy).then_inc(pt_ev, 1)

            def take_o(s):
                a.wait_ge(o_mm, s + 1)
                a.activation(aT[:, :, s * P:(s + 1) * P], bank[3][:].rearrange("p (j q) -> p j q", j=GROUP), ACT.Copy
                             ).then_inc(o_ev, 1)

            take_kv(0)
            take_q(0)
            for s in ATTN:
                if s + 1 < NT:
                    take_kv(s + 1)
                take_qT(s)
                if s >= 1:
                    take_PT(s - 1)
                if s + 1 < NT:
                    take_q(s + 1)
                if s >= 1:
                    take_o(s - 1)
                exps(s)
            take_PT(NT - 1)
            take_o(NT - 1)

            for i in range(2 * CT):
                h, c = divmod(i, CT)
                a.wait_ge(cen_done, i + 1)
                a.activation(sqT[:, c, h * HALF:(h + 1) * HALF], cT[:, c, h * HALF:(h + 1) * HALF], ACT.Square
                             ).then_inc(csq_done, 1)
            for h in range(2):
                a.wait_ge(lvar, h + 1)
                a.activation(rln[:, h, :], rln[:, h, :], ACT.Sqrt).then_inc(lrs, 1)
            for i in range(2 * CT):
                h, c = divmod(i, CT)
                a.wait_ge(cn_done, i + 1)
                if i >= 2:
                    a.wait_ge(mix_ready, i - 1)
                src = cT[:, c, h * HALF:(h + 1) * HALF]
                a.activation(sigl[:, i % 2, :], src, ACT.Sigmoid, bias=col(LB + c), scale=col(LG + c))
                a.activation(src, src, ACT.Identity, bias=col(LB + c), scale=col(LG + c)).then_inc(sil_act, 1)

            def h_square(t):
                a.wait_ge(h_ready, t + 1)
                if t >= 1:
                    a.wait_ge(h_sq, t)
                a.activation(hsq, hb[:, t % 4, :], ACT.Square, accum_out=ss[:, 2, t:t + 1]
                             ).then_inc(h_sq, 1)

            def take_vT(t):
                if t >= 1:
                    a.wait_ge(lg_mm, t)
                for b in range(2):
                    a.wait_ge(vt_mm, 2 * t + b + 1)
                    a.activation(vT[:, 4 * b:4 * b + 4, :], bank[4 + b][:].rearrange("p (k q) -> p k q", k=4),
                                 ACT.Copy).then_inc(vt_ev, 1)

            def gate_exp(t):
                a.wait_ge(lg_neg, t + 1)
                a.activation(eg[:], lg[:], ACT.Exp, bias=gs[:, 0:1]).then_inc(eg_ready, 1)

            def take_GT(t):
                a.wait_ge(gt_mm, t + 1)
                a.activation(GT[:], bank[7][0:NE, 0:P], ACT.Copy).then_inc(gt_ev, 1)

            for t in range(NT + 1):
                if 1 <= t <= NT:
                    take_vT(t - 1)
                if t >= 2:
                    take_GT(t - 2)
                if t < NT:
                    h_square(t)
                if 1 <= t <= NT:
                    gate_exp(t - 1)
            take_GT(NT - 1)

            a.sem_inc(yT_ev, 2)
            a.wait_ge(tab_ready, 1)
            n_pass = a.value_load(tabI[0:1, 128:129], min_val=NE, max_val=QMAX)
            with a.Fori(0, n_pass) as q:
                tier = a.value_load(tabI[0:1, ds(q + 64, 1)])
                by_tier(a, tier, lambda n: act_pass(a, q, n))

        OWN = 32

        def dve_pass(v, q, n, e, e_next, prep, one_hots, take_idx, take_xT):
            q8 = v.snap(q * 8)
            q32 = v.snap(q * OWN)
            own = [0]

            def link(ins):
                own[0] += 1
                ins.then_inc(dve_loop, 1)
                v.wait_ge(dve_loop, q32 + own[0])

            link(v.tensor_copy(b1c[:], b1T[:, ds(e * (2 * MT), 2 * MT)]))

            def hidden_a(m):
                r = m % 2
                if m >= 2:
                    v.wait_ge(act_ready, q8 + (m - 1))
                v.wait_ge(hid_mm, q8 + m + 1)
                v.tensor_scalar(g1[:, r, 0:n], bank[r][:, 0:n], b1c[:, m:m + 1], LIMIT, ALU.add, ALU.min
                                ).then_inc(g1_ready, 1)
                v.tensor_scalar(l1[:, r, 0:n], bank[r][:, SLOTS:SLOTS + n], b1c[:, MT + m:MT + m + 1], LIMIT + 1.0,
                                ALU.add, ALU.min).then_inc(hid_free, 1)

            def hidden_b(m):
                r = m % 2
                v.wait_ge(sg_ready, q8 + m + 1)
                own[0] += 1
                v.tensor_tensor(tt[:, r, 0:n], g1[:, r, 0:n], sg[:, r, 0:n], ALU.mult).then_inc(dve_loop, 1)
                v.wait_ge(dve_loop, q32 + own[0])
                v.sem_inc(sg_free, 1)
                v.scalar_tensor_tensor(act[:, m, 0:n], l1[:, r, 0:n], 1.0 - LIMIT, tt[:, r, 0:n], ALU.max, ALU.mult
                                       ).then_inc(act_ready, 1)

            hidden_a(0)
            for m in range(1, MT):
                hidden_a(m)
                hidden_b(m - 1)
                if m == 1:
                    link(prep(rank[:, :, ds(e_next, 1)].rearrange("p t o -> p (t o)"), baseB[:, ds(q + 1, 1)]))
                    one_hots()
                if m == 3:
                    for i in range(2):
                        v.wait_ge(added[i], q * 16 + 16)
                    v.wait_ge(gath_in, q * 32 + 32)
                    v.tensor_copy(idx_cur[:], idx_next[:])
                    link(v.tensor_copy(gate_cur[:], gath[:, :, ds(e + D, 1)].rearrange("p h o -> p (h o)")))
                    v.sem_inc(cur_ready, 1)
                if m == 4:
                    v.wait_ge(idx_mm, q + 2)
                    first, second = take_idx()
                    link(first)
                    second().then_inc(idx_ready, 1)
            hidden_b(MT - 1)
            q4 = v.snap(q * 4 + 4)
            for i in range(4):
                take_xT(q4, i)
            v.sem_inc(dve_loop, OWN - own[0])

        @block.vector
        def _(v):
            own = [0]

            def link(ins):
                own[0] += 1
                ins.then_inc(dve_own, 1)
                v.wait_ge(dve_own, own[0])

            for t in range(NT):
                v.wait_ge(xrs, t + 1)
                v.tensor_scalar(xin[:, t, :], xin[:, t, :], rs[:, 0, t:t + 1], None, ALU.mult).then_inc(u_ready, 1)
                if t == 0:
                    v.wait_ge(cols_mm, 1)
                    v.tensor_copy(cols[:, 0:30], bank[4][:, 0:30])
                    v.tensor_copy(cols[:, CW:CW + CT * WIDTH], bank[4][:, CW:CW + CT * WIDTH]).then_inc(cols_done, 1)
            v.wait_ge(cols_done, 1)
            for g in range(1, 2 * KD, 2):
                h, k = divmod(g, KD)
                v.wait_ge(ut_mm, g + 1)
                v.tensor_scalar(uT[:, k, h * HALF:(h + 1) * HALF], bank[7][:], col(G1 + k), None, ALU.mult
                                ).then_inc(ut_dve, 1)
            v.wait_ge(b1_mm, 1)
            link(v.tensor_copy(b1T[:], bank[5][:]))
            b1v = b1T[:].rearrange("p (e s) -> p e s", e=NE)
            v.tensor_scalar_add(b1v[:, :, MT:], b1v[:, :, MT:], 1.0)
            for k in range(KD):
                last = v.tensor_scalar(rw[:, k, :], rw[:, k, :], col(G2 + k), None, ALU.mult)
            last.then_inc(b1_done, 1)

            taps = [(c, j) for c in range(1, CT) for j in range(WIDTH)]

            def tap(c, j):
                if j == 0:
                    v.wait_ge(z_ready, 2 * (c + 1))
                    link(v.tensor_scalar(cT[:, c, :], zT[:, c, 0:SEQ], col(CW + c * WIDTH), col(CB + c),
                                         ALU.mult, ALU.add))
                else:
                    link(v.scalar_tensor_tensor(cT[:, c, :], zT[:, c, j:j + SEQ], col(CW + c * WIDTH + j),
                                                cT[:, c, :], ALU.mult, ALU.add))

            def some_taps(n):
                for c, j in taps[:n]:
                    tap(c, j)
                del taps[:n]

            def norm_qk(s):
                v.wait_ge(q_ev, s + 1)
                v.tensor_reduce(ss[:, 1, 0:10], sq.rearrange("p (h d) -> p h d", d=HD), AX.X, ALU.add
                                ).then_inc(hss, 1)
                some_taps(1)
                v.wait_ge(hrs, s + 1)
                if s >= 1:
                    v.wait_ge(qt_mm, s)
                r = rs[:, 1, 0:10]
                v.tensor_tensor(qn[:, 0:GROUP], qs[:, 0:HALF].rearrange("p (g j d) -> p j g d", g=NKV, j=GROUP),
                                r[:, 0:NH].rearrange("p (g j) -> p j g", g=NKV).unsqueeze(3)
                                .to_broadcast([P, GROUP, NKV, HD]), ALU.mult)
                v.tensor_tensor(qn[:, GROUP], qs[:, HALF:HALF + P].rearrange("p (g d) -> p g d", g=NKV),
                                r[:, NH:10].unsqueeze(2).to_broadcast([P, NKV, HD]), ALU.mult).then_inc(qn_ready, 1)

            def softmax_a(s):
                m = (mask_first if s == 0 else mask_rest).unsqueeze(1).to_broadcast([P, 2, WIN])
                if s >= 1:
                    v.wait_ge(p_ready, s)
                for b in range(4):
                    v.wait_ge(s_mm, 4 * s + b + 1)
                    ins = v.scalar_tensor_tensor(S[:, 2 * b:2 * b + 2, :],
                                                 bank[b][:, 0:2 * WIN].rearrange("p (h w) -> p h w", h=2),
                                                 HD ** -0.5, m, ALU.mult, ALU.add)
                    ins.then_inc(s_ev, 1)
                v.wait_ge(s_ev, 4 * s + 4)
                link(v.tensor_reduce(mx[:], S, AX.X, ALU.max))
                link(v.tensor_tensor(mx[:], mx[:], sink[:], ALU.max))
                v.tensor_scalar_mul(nmx[:], mx[:], -1.0)
                v.tensor_tensor(sd[:], sink[:], mx[:], ALU.subtract).then_inc(m_ready, 1)

            def softmax_b(s):
                v.wait_ge(e_ready, s + 1)
                link(v.tensor_tensor(den[:], den[:], es[:], ALU.add))
                link(v.reciprocal(rden[:], den[:]))
                if s >= 1:
                    v.wait_ge(pt_mm, 3 * s)
                v.tensor_tensor(prob[:, :, CHUNK:], S, rden[:].unsqueeze(2).to_broadcast([P, NH, WIN]), ALU.mult
                                ).then_inc(p_ready, 1)

            some_taps(WIDTH + 18)
            norm_qk(0)
            v.wait_ge(tap_added, WIDTH - 1)
            for s in ATTN:
                some_taps(1)
                if s + 1 < NT:
                    norm_qk(s + 1)
                if s + 1 == NT:
                    some_taps(len(taps))
                    v.sem_inc(conv_done, 1)
                softmax_a(s)
                some_taps(2)
                softmax_b(s)
                some_taps(2)

            for i in range(2 * CT):
                h, c = divmod(i, CT)
                v.wait_ge(mean_mm, h + 1)
                t_ = cT[:, c, h * HALF:(h + 1) * HALF]
                v.tensor_tensor(t_, t_, bank[6 + h][:], ALU.subtract).then_inc(cen_done, 1)
            for h in range(2):
                v.wait_ge(var_mm, h + 1)
                v.tensor_scalar_add(rln[:, h, :], bank[6 + h][:], EPS).then_inc(lvar, 1)
            for i in range(2 * CT):
                h, c = divmod(i, CT)
                if c == 0:
                    v.wait_ge(lrs, h + 1)
                    link(v.reciprocal(rln[:, h, :], rln[:, h, :]))
                t_ = cT[:, c, h * HALF:(h + 1) * HALF]
                v.tensor_tensor(t_, t_, rln[:, h, :], ALU.mult).then_inc(cn_done, 1)
            for i in range(2 * CT):
                h, c = divmod(i, CT)
                v.wait_ge(sil_act, i + 1)
                t_ = cT[:, c, h * HALF:(h + 1) * HALF]
                v.tensor_tensor(t_, t_, sigl[:, i % 2, :], ALU.mult).then_inc(mix_ready, 1)

            def residual(t):
                v.wait_ge(xh_in[t % 2], 16 * (t // 2 + 1))
                if t >= 4:
                    v.wait_ge(h_out[t % 4], 16 * (t // 4))
                for b in range(2):
                    v.wait_ge(wo_mm, 2 * t + b + 1)
                    last = v.tensor_tensor(hb[:, t % 4, b * HALF:(b + 1) * HALF], bank[mixed_bank(t) + b][:],
                                           xh[:, t % 2, b * HALF:(b + 1) * HALF], ALU.add)
                last.then_inc(h_ready, 1)

            def norm_v(t):
                v.wait_ge(h_rs, t + 1)
                if t >= 2:
                    v.wait_ge(row_out[t % 2], 16 * (t // 2))
                v.tensor_scalar(vrow[:, t % 2, 0:D], hb[:, t % 4, :], rs[:, 2, t:t + 1], None, ALU.mult
                                ).then_inc(v_ready, 1)

            def route(t):
                v.wait_ge(lg_mm, t + 1)
                link(v.tensor_tensor(lg[:], bank[6][:, 0:NE], rb[:], ALU.add))
                link(v.max(top8[:], lg[:]))
                v.tensor_scalar_mul(gs[:, 0:1], top8[:, 0:1], -1.0).then_inc(lg_neg, 1)
                link(v.max_index(ix8[:], top8[:], lg[:]))
                link(v.tensor_copy(ixf[:], ix8[:]))
                link(v.tensor_scalar(mk[:, 0, :], iota_e[:], ixf[:, 0:1], None, ALU.is_equal))
                for k in range(1, TOPK):
                    dst = Mf[:, t, :] if k == TOPK - 1 else mk[:, k % 2, :]
                    link(v.scalar_tensor_tensor(dst, iota_e[:], ixf[:, k:k + 1], mk[:, (k - 1) % 2, :],
                                                ALU.is_equal, ALU.add))
                v.tensor_copy(Mb[:, t, :], Mf[:, t, :]).then_inc(mask_ready, 1)
                v.wait_ge(eg_ready, t + 1)
                link(v.tensor_tensor(gg[:], eg[:], Mf[:, t, :], ALU.mult))
                link(v.tensor_reduce(gs[:, 1:2], gg[:], AX.X, ALU.add))
                link(v.reciprocal(gs[:, 2:3], gs[:, 1:2]))
                v.tensor_scalar(vrow[:, t % 2, D:ROW], gg[:], gs[:, 2:3], None, ALU.mult).then_inc(gate_ready, 1)

            def add_b2(t):
                v.wait_ge(b2_mm, t + 1)
                for b in range(2):
                    t_ = hb[:, t % 4, b * HALF:(b + 1) * HALF]
                    last = v.tensor_tensor(t_, t_, bank[4 + b][:], ALU.add)
                last.then_inc(h2_ready, 1)

            for t in range(NT + 1):
                if t < NT:
                    residual(t)
                    norm_v(t)
                if 1 <= t <= NT:
                    route(t - 1)
                if t >= 2:
                    add_b2(t - 2)

            v.wait_ge(rank_mm, 1)
            v.tensor_copy(pos[:].rearrange("p t e -> p (t e)"), bank[0][:, 0:NT * NE])
            link(v.tensor_copy(nE[:], bank[0][:, NT * NE:NT * NE + NE]))
            link(v.tensor_tensor(rka[:], tokid[:].unsqueeze(2).to_broadcast([P, NT, NE]), pos[:], ALU.subtract))
            link(v.tensor_tensor(rka[:], rka[:], nE[:].unsqueeze(1).to_broadcast([P, NT, NE]), ALU.add))
            link(v.tensor_tensor(rkd[:], pos[:], rka[:], ALU.subtract))
            link(v.tensor_tensor(rkd[:], rkd[:], Mf[:], ALU.mult))
            link(v.tensor_tensor(rank[:], rka[:], rkd[:], ALU.add))

            def prep(ranks, base):
                return v.tensor_scalar(r8[:], ranks, base, None, ALU.subtract)

            def one_hots():
                for t in range(NT):
                    last = v.tensor_scalar(onehot[:, t, :], iota_s[:], r8[:, t:t + 1], None, ALU.is_equal)
                last.then_inc(oh_ready, 1)

            link(prep(rank[:, :, 0], 0.0))
            one_hots()
            add_b2(NT - 1)

            def take_idx():
                halves = idf[:].rearrange("p (h c) -> p c h", c=2)
                return v.tensor_copy(idf[:], bank[6][:, 0:4]), lambda: v.scalar_tensor_tensor(
                    idx_next[:], halves[:, 0], float(P), halves[:, 1], ALU.mult, ALU.add)

            v.wait_ge(idx_mm, 1)
            first, second = take_idx()
            link(first)
            second().then_inc(idx_ready, 1)

            link(v.memset(cum[:], 0.0))
            link(v.tensor_scalar(tb[:, 0, :], nE[:], float(SLOTS), 1.0, ALU.is_gt, ALU.add))
            link(v.scalar_tensor_tensor(tb[:, 1, :], nE[:], 2.0 * SLOTS, tb[:, 0, :], ALU.is_gt, ALU.add))
            link(v.scalar_tensor_tensor(cum[:, 0, 16:], nE[:], 3.0 * SLOTS, tb[:, 1, :], ALU.is_gt, ALU.add))
            for i in range(5):
                k = 1 << i
                link(v.tensor_tensor(cum[:, (i + 1) % 2, 16:], cum[:, i % 2, 16:], cum[:, i % 2, 16 - k:16 + NE - k],
                                     ALU.add))
            last_pass = cum[:, 1, 16:]
            link(v.tensor_scalar(tb[:, 0, :], last_pass, qcol[:], None, ALU.is_le))
            link(v.tensor_tensor(tb[:, 1, :], tb[:, 0, :], last_pass, ALU.mult))
            v.tensor_reduce(tc[:, 0:1], tb[:, 0, :], AX.X, ALU.add)
            link(v.tensor_reduce(tc[:, 1:2], tb[:, 1, :], AX.X, ALU.max))
            link(v.tensor_scalar(tb[:, 0, :], iota_e[:], tc[:, 0:1], None, ALU.is_equal))
            link(v.tensor_tensor(tb[:, 1, :], tb[:, 0, :], nE[:], ALU.mult))
            v.tensor_reduce(tc[:, 2:3], tb[:, 1, :], AX.X, ALU.add)
            link(v.tensor_tensor(tc[:, 3:4], qcol[:], tc[:, 1:2], ALU.subtract))
            link(v.tensor_scalar_mul(tc[:, 3:4], tc[:, 3:4], float(SLOTS)))
            link(v.tensor_tensor(tc[:, 4:5], tc[:, 2:3], tc[:, 3:4], ALU.subtract))
            link(v.tensor_scalar(tb[:, 0, 0:len(TIERS) - 1], limits[:], tc[:, 4:5], None, ALU.is_lt))
            link(v.tensor_reduce(tc[:, 5:6], tb[:, 0, 0:len(TIERS) - 1], AX.X, ALU.add))
            link(v.tensor_scalar_min(tc[:, 0:1], tc[:, 0:1], float(NE - 1)))
            for i, c in enumerate((0, 5, 3)):
                last = v.tensor_scalar(diag[:, i, :], ident[:, 0:64], tc[:, c:c + 1], None, ALU.mult)
            last.then_inc(diag_ready, 1)
            v.wait_ge(tab_mm, 1)
            v.tensor_copy(tabI[:, 0:128], bank[1][:, 0:128])
            v.tensor_copy(baseB[:], bank[1][:, 128:192])
            v.tensor_copy(tabI[:, 128:129], last_pass[:, NE - 1:NE]).then_inc(tab_ready, 1)

            def take_xT(before, i):
                v.wait_ge(xt_mm, before + i + 1)
                for k in (2 * i, 2 * i + 1):
                    last = v.tensor_scalar(xT[:, k, :], bank[6][:, (k % 2) * SLOTS:(k % 2 + 1) * SLOTS],
                                           col(G2 + k), None, ALU.mult)
                last.then_inc(xt_ev, 1)

            for i in range(4):
                take_xT(0, i)

            v.sem_inc(hid_free, 2)
            v.sem_inc(sg_free, 2)
            for i in range(4):
                v.wait_ge(h_out[i], 16 * (NT // 4))
            v.wait_ge(tab_ready, 1)
            n_pass = v.value_load(tabI[0:1, 128:129], min_val=NE, max_val=QMAX)
            with v.Fori(0, n_pass) as q:
                tier = v.value_load(tabI[0:1, ds(q + 64, 1)])
                e = v.value_load(tabI[0:1, ds(q, 1)])
                e_next = v.value_load(tabI[0:1, ds(q + 1, 1)])
                by_tier(v, tier, lambda n: dve_pass(v, q, n, e, e_next, prep, one_hots, take_idx, take_xT))

        def pe_pass(pe, q, n, slots_to_tokens, trans_x):
            mm = pe.matmul
            q2, q4, q8 = pe.snap(q * 2), pe.snap(q * 4 + 4), pe.snap(q * 8)
            q16, q32 = pe.snap(q * 16 + 16), pe.snap(q * 32 + 32)
            pe.wait_ge(xt_ev, q4)
            for m in range(MT):
                if m % 2 == 0:
                    pe.wait_ge(w1_in[m // 2], q32)
                pe.wait_ge(hid_free, q8 + m + 1)
                for side in range(2):
                    lo = side * FF + m * P
                    for k in range(KD):
                        last = mm(bank[m % 2][:, side * SLOTS:side * SLOTS + n], w1_sb[:, k, lo:lo + P],
                                  xT[:, k, 0:n], start=k == 0, stop=k == KD - 1)
                last.then_inc(hid_mm, 1)
                if m == 3:
                    slots_to_tokens(q + 2)

            def down(d, ms):
                if 0 in ms:
                    if d % 4 == 0:
                        pe.wait_ge(w2_in[d // 4], q16)
                    pe.wait_ge(yT_ev, q8 + d + 1)
                for m in ms:
                    if d == 0 or (d == 1 and m == MT - 1):
                        pe.wait_ge(act_ready, q8 + m + 1)
                    last = mm(bank[2 + d % 2][:, 0:n], w2_sb[:, m, d * P:(d + 1) * P], act[:, m, 0:n],
                              start=m == 0, stop=m == MT - 1)
                if MT - 1 in ms:
                    last.then_inc(y_mm, 1)

            def trans_y(d):
                pe.wait_ge(yT_ev, q8 + d + 3)
                if d == 0:
                    pe.wait_ge(yt_ev, q2)
                if d == 4:
                    pe.wait_ge(yt_ev, q2 + 1)
                c = (d % 4) * P
                w = min(n, P)
                last = pe.transpose(bank[4 + d // 4][0:w, c:c + P], yT[:, d, 0:w], ident[:])
                if n > P:
                    last = pe.transpose(bank[7][0:n - P, c:c + P], yT[:, d, P:n], ident[:])
                if d % 4 == 3:
                    last.then_inc(yt_mm, 1)

            down(0, range(MT - 1))
            down(1, range(MT - 1))
            down(0, [MT - 1])
            pe.wait_ge(gath_in, q32 + 32)
            pe.wait_ge(idx_ready, q + 2)
            trans_x(q4, 0)
            down(1, [MT - 1])
            down(2, range(MT))
            trans_y(0)
            down(3, range(MT))
            trans_y(1)
            trans_x(q4, 1)
            down(4, range(MT))
            trans_y(2)
            down(5, range(MT))
            trans_y(3)
            trans_x(q4, 2)
            down(6, range(MT))
            trans_y(4)
            trans_x(q4, 3)
            down(7, range(MT))
            trans_y(5)
            trans_y(6)
            trans_y(7)

        @block.tensor
        def _(pe):
            mm = pe.matmul
            pe.wait_ge(ident_ready, 1)
            pe.wait_ge(rows_in, 16 * N_ROWS)
            pe.transpose(bank[4][:, 0:30], rows30[0:30, :], ident[0:30, 0:30])
            for c in range(CT):
                last = pe.transpose(bank[4][:, CW + c * WIDTH:CW + (c + 1) * WIDTH], rows_cw[0:WIDTH, c * P:(c + 1) * P],
                                    ident[0:WIDTH, 0:WIDTH])
            last.then_inc(cols_mm, 1)
            for g in range(2 * KD):
                h, k = divmod(g, KD)
                if k == 0:
                    pe.wait_ge(u_ready, 4 * (h + 1))
                if g >= 2:
                    pe.wait_ge(ut_act if g % 2 == 0 else ut_dve, g // 2)
                for t in range(4):
                    last = pe.transpose(bank[6 + g % 2][:, t * P:(t + 1) * P], xin[:, 4 * h + t, k * P:(k + 1) * P],
                                        ident[:])
                last.then_inc(ut_mm, 1)
            pe.wait_ge(wcv_in, 32)
            for i in range(2 * CT):
                c, h = divmod(i, 2)
                if i < 2:
                    pe.wait_ge(ut_act, KD // 2 * (h + 1))
                    pe.wait_ge(ut_dve, KD // 2 * (h + 1))
                if i >= 2:
                    pe.wait_ge(glu_ev, 2 * (i - 1))
                for side in range(2):
                    for k in range(KD):
                        lo = side * D_CONV + c * P
                        last = mm(bank[2 * (i % 2) + side][:], w_cv[:, k, lo:lo + P], uT[:, k, h * HALF:(h + 1) * HALF],
                                  start=k == 0, stop=k == KD - 1)
                last.then_inc(glu_mm, 1)
                if i == 1:
                    pe.wait_ge(small_in, 16 * N_SMALL)
                    for g in range(4):
                        last = pe.transpose(bank[5][:, g * P:(g + 1) * P], rows_b1[:, g, :], ident[:])
                    last.then_inc(b1_mm, 1)

            def proj_q(s, ks=range(KD)):
                if s == 0:
                    pe.wait_ge(wqkv_in, 16)
                    pe.wait_ge(cols_done, 1)
                else:
                    pe.wait_ge(q_ev, s)
                for k in ks:
                    last = mm(bank[4][:], uT[:, k, s * P:(s + 1) * P], w_qkv[:, k, 0:HALF], start=k == 0,
                              stop=k == KD - 1)
                if KD - 1 in ks:
                    last.then_inc(q_mm, 1)

            def proj_kv(s):
                if s == 0:
                    pe.wait_ge(wqkv_in, 16)
                    pe.wait_ge(b1_done, 1)
                else:
                    pe.wait_ge(kv_ev, s)
                for k in range(KD):
                    last = mm(bank[5][:, 0:2 * P], uT[:, k, s * P:(s + 1) * P], w_qkv[:, k, HALF:QKV], start=k == 0,
                              stop=k == KD - 1)
                last.then_inc(kv_mm, 1)

            def trans_q(s):
                pe.wait_ge(qn_ready, s + 1)
                if s >= 1:
                    pe.wait_ge(qt_ev, s)
                flat = qn.rearrange("p j g d -> p j (g d)")
                for j in range(GROUP):
                    pe.transpose(bank[6][:, j * P:(j + 1) * P], flat[:, j, :], ident[:])
                pe.transpose(bank[7][:, 0:P], flat[:, GROUP, :], ident[:]).then_inc(qt_mm, 1)

            def scores(s):
                pe.wait_ge(qt_ev, s + 1)
                if s == 0:
                    pe.wait_ge(glu_ev, 4 * CT)
                for b in range(4):
                    if s >= 1 and b < 3:
                        pe.wait_ge(pt_ev, 3 * (s - 1) + b + 1)
                    if s >= 1 and b == 3:
                        pe.wait_ge(o_ev, s)
                    for h in (2 * b, 2 * b + 1):
                        g, j = divmod(h, GROUP)
                        last = mm(bank[b][:, (h % 2) * WIN:(h % 2 + 1) * WIN], qT[g * HD:(g + 1) * HD, j, :],
                                  kT[g * HD:(g + 1) * HD, s * P:s * P + WIN], start=True, stop=True)
                    last.then_inc(s_mm, 1)

            def trans_p(s):
                pe.wait_ge(p_ready, s + 1)
                for g in range(NKV):
                    for j in range(GROUP):
                        last = pe.transpose(bank[g][:, j * P:(j + 1) * P], prob[:, g * GROUP + j, P:2 * P], ident[:])
                    last.then_inc(pt_mm, 1)
                for h in range(NH):
                    last = pe.transpose(bank[2][:, h * CHUNK:(h + 1) * CHUNK], prob[0:CHUNK, h, 0:P],
                                        ident[0:CHUNK, 0:CHUNK])
                last.then_inc(pt_mm, 1)

            def weigh_v(s):
                pe.wait_ge(pt_ev, 3 * s + 3)
                for g in range(NKV):
                    o = bank[3][g * HD:(g + 1) * HD, :]
                    last = mm(o, vv[:, s, g * HD:(g + 1) * HD], PTc[:, g * GROUP:(g + 1) * GROUP, :],
                              start=True, stop=s == 0)
                    if s >= 1:
                        last = mm(o.rearrange("p (j q) -> p j q", j=GROUP)[:, :, 0:CHUNK],
                                  vv[:, s - 1, g * HD:(g + 1) * HD], PTp[:, g * GROUP:(g + 1) * GROUP, :],
                                  start=False, stop=True)
                last.then_inc(o_mm, 1)

            def out_half(t, part_):
                if part_ == 0:
                    if t == 0:
                        pe.wait_ge(wo_in, 48)
                        pe.wait_ge(q_ev, NT)
                        pe.wait_ge(kv_ev, NT)
                        pe.wait_ge(o_ev, 1)
                    if t == 1:
                        pe.wait_ge(pt_ev, 3 * NT)
                        pe.wait_ge(o_ev, NT)
                    if t >= 3:
                        pe.wait_ge(h_ready, t - 1)
                for b in range(2):
                    for i in range(CT):
                        src = (aT if part_ == 0 else cT)[:, i, t * P:(t + 1) * P]
                        k = i + (CT if part_ == 0 else 0)
                        last = mm(bank[mixed_bank(t) + b][:], src, w_o[:, k, b * HALF:(b + 1) * HALF],
                                  start=part_ == 0 and i == 0, stop=part_ == 1 and i == CT - 1)
                    if part_ == 1:
                        last.then_inc(wo_mm, 1)

            proj_kv(0)
            proj_q(0)
            for s in ATTN:
                if s + 1 < NT:
                    proj_kv(s + 1)
                trans_q(s)
                if s + 1 < NT:
                    proj_q(s + 1, range(KD - 2))
                if s == NT - 1:
                    out_half(0, 0)
                if s >= 1:
                    trans_p(s - 1)
                if s + 1 < NT:
                    proj_q(s + 1, [KD - 2, KD - 1])
                if s >= 1:
                    weigh_v(s - 1)
                scores(s)

            def channel_sum(src, ready, done):
                for h in range(2):
                    ready(h)
                    for c in range(CT):
                        last = mm(bank[6 + h][:], ones_ln[:], src[:, c, h * HALF:(h + 1) * HALF], start=c == 0,
                                  stop=c == CT - 1)
                    last.then_inc(done, 1)

            pe.wait_ge(consts, 1)
            pe.wait_ge(conv_done, 1)
            channel_sum(cT, lambda h: pe.wait_ge(qt_ev, NT), mean_mm)
            trans_p(NT - 1)
            weigh_v(NT - 1)

            channel_sum(sqT, lambda h: pe.wait_ge(csq_done, CT * (h + 1)), var_mm)
            out_half(1, 0)
            out_half(2, 0)

            def trans_gates(u):
                pe.wait_ge(gate_ready, u + 1)
                pe.wait_ge(lvar, 2)
                pe.transpose(bank[7][0:NE, 0:P], vrow[:, u % 2, D:ROW], ident[:]).then_inc(gt_mm, 1)

            def gates_b2(u):
                if u == 0:
                    pe.wait_ge(b2_in, 16)
                else:
                    pe.wait_ge(h2_ready, u)
                pe.wait_ge(vt_ev, 2 * min(u + 2, NT))
                pe.wait_ge(gt_ev, u + 1)
                for b in range(2):
                    last = mm(bank[4 + b][:], GT[:], b2_sb[:, b * HALF:(b + 1) * HALF], start=True, stop=True)
                last.then_inc(b2_mm, 1)

            for t in range(NT + 1):
                if t < NT:
                    if t >= 3:
                        out_half(t, 0)
                if 1 <= t <= NT:
                    u = t - 1
                    pe.wait_ge(v_ready, u + 1)
                    if u >= 2:
                        pe.wait_ge(h2_ready, u - 1)
                    if u == 0:
                        pe.wait_ge(q_ev, NT)
                    for b in range(2):
                        if u >= 1:
                            pe.wait_ge(vt_ev, 2 * u)
                        for k in range(4):
                            c = 4 * b + k
                            last = pe.transpose(bank[4 + b][:, k * P:(k + 1) * P],
                                                vrow[:, u % 2, c * P:(c + 1) * P], ident[:])
                        last.then_inc(vt_mm, 1)
                if t < NT:
                    if t == 0:
                        pe.wait_ge(mix_ready, CT)
                    if t == NT // 2:
                        pe.wait_ge(mix_ready, 2 * CT)
                    out_half(t, 1)
                if t >= 2:
                    trans_gates(t - 2)
                if 1 <= t <= NT:
                    u = t - 1
                    pe.wait_ge(vt_ev, 2 * u + 2)
                    if u == 0:
                        pe.wait_ge(lvar, 2)
                    else:
                        pe.wait_ge(lg_neg, u)
                    for k in range(KD):
                        last = mm(bank[6][:, 0:NE], vT[:, k, :], rw[:, k, :], start=k == 0, stop=k == KD - 1)
                    last.then_inc(lg_mm, 1)
                if t >= 2:
                    gates_b2(t - 2)

            pe.wait_ge(mask_ready, NT)
            pe.wait_ge(h_ready, NT)
            for t in range(NT + 1):
                for u in range(min(t, NT - 1) + 1):
                    own_tile = u == t
                    last = mm(bank[0][:, t * NE:(t + 1) * NE], tri_b[:] if own_tile else ones_b[:], Mb[:, u, :],
                              start=u == 0, stop=u == min(t, NT - 1))
            last.then_inc(rank_mm, 1)

            def slots_to_tokens(n):
                pe.wait_ge(oh_ready, n)
                for h in range(2):
                    for t in range(NT):
                        last = mm(bank[6][:, 2 * h:2 * h + 2], onehot[:, t, h * P:(h + 1) * P], tokcode[:, t, :],
                                  start=t == 0, stop=t == NT - 1)
                last.then_inc(idx_mm, 1)

            def trans_x(before, i):
                if i >= 1:
                    pe.wait_ge(xt_ev, before + i)
                for k in (2 * i, 2 * i + 1):
                    for h in range(2):
                        last = pe.transpose(bank[6][:, (k % 2) * SLOTS + h * P:(k % 2) * SLOTS + (h + 1) * P],
                                            gath[:, h, k * P:(k + 1) * P], ident[:])
                last.then_inc(xt_mm, 1)

            trans_gates(NT - 1)
            gates_b2(NT - 1)
            slots_to_tokens(1)
            pe.wait_ge(diag_ready, 1)
            mm(bank[1][:, 0:192], ones_f[:], diag[:].rearrange("p a b -> p (a b)"), start=True, stop=True
               ).then_inc(tab_mm, 1)
            pe.wait_ge(gath_in, 32)
            for i in range(4):
                trans_x(0, i)
            pe.wait_ge(h2_ready, NT)

            pe.wait_ge(tab_ready, 1)
            n_pass = pe.value_load(tabI[0:1, 128:129], min_val=NE, max_val=QMAX)
            with pe.Fori(0, n_pass) as q:
                tier = pe.value_load(tabI[0:1, ds(q + 64, 1)])
                by_tier(pe, tier, lambda n: pe_pass(pe, q, n, slots_to_tokens, trans_x))


_INS = ["x", "norm1_g", "w_in", "conv_w", "conv_b", "conv_ln_g", "conv_ln_b", "q_norm_g", "k_norm_g", "sinks",
        "w_out", "norm2_g", "router_w", "router_b", "w1", "b1", "w2", "b2"]


def kernel(**inputs):
    import concourse.bacc as bacc
    from concourse.bass_utils import run_bass_kernel_spmd

    nc = bacc.Bacc("TRN2", target_bir_lowering=False, num_devices=1)
    arrays, args = {}, []
    for name in _INS:
        a = np.ascontiguousarray(inputs[name])
        arrays[f"in_{name}"] = a
        args.append(nc.dram_tensor(f"in_{name}", a.shape, mybir.dt.from_np(a.dtype), kind="ExternalInput").ap())
    out = nc.dram_tensor("out", (1, SEQ, D), mybir.dt.float32, kind="ExternalOutput").ap()
    hybrid_block(nc, *args, out)
    r = run_bass_kernel_spmd(nc, [arrays], core_ids=[0])
    return r.results[0]["out"]
```
